# Optimizing a Trainium2 kernel written in Bass

```python
import jax, jax.numpy as jnp
from jax import lax
import numpy as np

D_MODEL = 1024
BATCH = 1
SEQ = 512
DEPTH = 2
DEC_BATCH = 1
DEC_SEQ = 64
PAST_LEN = 256

CHUNK = 64
EPS = 1e-6
ROPE_THETA = 10000.0
D_FF = 2816
NEG = -1e30
MLP_CHUNK = 128
A_GROUPS = 4
A_GDIM = 64
A_WIDTH = A_GROUPS * A_GDIM
B_HEADS = 8
B_KV_HEADS = 2
B_HEAD_DIM = 64
B_GROUP = B_HEADS // B_KV_HEADS
B_Q = B_HEADS * B_HEAD_DIM
B_KV = B_KV_HEADS * B_HEAD_DIM
WINDOW = 128
C_HEADS = 4
C_Q_LORA = 384
C_KV_LORA = 128
C_NOPE = 64
C_ROPE = 32
C_V = 64
MLA_Q_BLOCK = 128
SPLIT_SIZES = (A_WIDTH, A_WIDTH, B_Q, B_KV, B_KV, C_Q_LORA, C_KV_LORA, C_ROPE)
D_IN = sum(SPLIT_SIZES)
D_MIX = A_WIDTH + B_Q + C_HEADS * C_V

kernel_name = "hymba_chunk_stream_encoder_step"

def rmsnorm(x, g):
    xf = x.astype(jnp.float32)
    y = xf * lax.rsqrt(jnp.mean(xf * xf, axis=-1, keepdims=True) + EPS)
    return (y * g.astype(jnp.float32)).astype(x.dtype)

def rope(x, pos):
    d = x.shape[-1]
    half = d // 2
    inv = ROPE_THETA ** (-2.0 * jnp.arange(half, dtype=jnp.float32) / d)
    ang = pos.astype(jnp.float32)[:, None] * inv[None, :]
    cos = jnp.cos(ang)[:, None, :]
    sin = jnp.sin(ang)[:, None, :]
    xf = x.astype(jnp.float32)
    x1, x2 = xf[..., :half], xf[..., half:]
    return jnp.concatenate([x1 * cos - x2 * sin, x2 * cos + x1 * sin], axis=-1).astype(x.dtype)

def ffn_half(x, g, wg, wu, wd):
    h = rmsnorm(x, g)
    return x + 0.5 * ((jax.nn.silu(h @ wg) * (h @ wu)) @ wd)

def split_proj(z):
    offs = [int(o) for o in np.cumsum(SPLIT_SIZES)[:-1]]
    return jnp.split(z, offs, axis=-1)

def chunk_mask(n):
    i = jnp.arange(n)
    return (i[None, :] // CHUNK) <= (i[:, None] // CHUNK)

def chunk_mlp_prompt(u, v, ws, bs):
    B, S, _ = v.shape
    n = S // MLP_CHUNK
    w = jnp.where(chunk_mask(MLP_CHUNK)[None], ws, 0.0).astype(v.dtype)
    vb = v.reshape(B, n, MLP_CHUNK, A_GROUPS, A_GDIM)
    mixed = jnp.einsum('gij,bnjgc->bnigc', w, vb) + bs.T[None, None, :, :, None]
    return u * mixed.reshape(B, S, A_WIDTH)

def chunk_mlp_sample(u, v, ws, bs):
    B, T, _ = v.shape
    w = jnp.where(chunk_mask(T)[None], ws[:, :T, :T], 0.0).astype(v.dtype)
    vb = v.reshape(B, T, A_GROUPS, A_GDIM)
    mixed = jnp.einsum('gij,bjgc->bigc', w, vb) + bs[:, :T].T[None, :, :, None]
    return u * mixed.reshape(B, T, A_WIDTH)

def attend_sinks(q, k, v, sink, valid):
    s = jnp.einsum('...qhgd,...khd->...hgqk', q, k).astype(jnp.float32) * (B_HEAD_DIM ** -0.5)
    if valid is not None:
        s = jnp.where(valid, s, NEG)
    sk = sink.astype(jnp.float32).reshape(B_KV_HEADS, B_GROUP)[:, :, None, None]
    m = jnp.maximum(jnp.max(s, axis=-1, keepdims=True), sk)
    p = jnp.exp(s - m)
    den = jnp.sum(p, axis=-1, keepdims=True) + jnp.exp(sk - m)
    return jnp.einsum('...hgqk,...khd->...qhgd', (p / den).astype(v.dtype), v)

def swa_prompt(q, k, v, sink):
    B, S = q.shape[:2]
    n = S // CHUNK
    wc = WINDOW // CHUNK
    qb = q.reshape(B, n, CHUNK, B_KV_HEADS, B_GROUP, B_HEAD_DIM)
    pad = ((0, 0), (wc * CHUNK, 0), (0, 0), (0, 0))
    kp = jnp.pad(k, pad).reshape(B, n + wc, CHUNK, B_KV_HEADS, B_HEAD_DIM)
    vp = jnp.pad(v, pad).reshape(B, n + wc, CHUNK, B_KV_HEADS, B_HEAD_DIM)
    kb = jnp.concatenate([kp[:, j:j + n] for j in range(wc + 1)], axis=2)
    vb = jnp.concatenate([vp[:, j:j + n] for j in range(wc + 1)], axis=2)
    kpos = (jnp.arange(n)[:, None] - wc) * CHUNK + jnp.arange((wc + 1) * CHUNK)[None, :]
    valid = (kpos >= 0)[None, :, None, None, None, :]
    o = attend_sinks(qb, kb, vb, sink, valid)
    return o.reshape(B, S, B_Q)

def swa_sample(q, k, v, ck, cv, sink):
    B, T = q.shape[:2]
    qb = q.reshape(B, T, B_KV_HEADS, B_GROUP, B_HEAD_DIM)
    kk = jnp.concatenate([ck, k], axis=1)
    vv = jnp.concatenate([cv, v], axis=1)
    return attend_sinks(qb, kk, vv, sink, None).reshape(B, T, B_Q)

def mla_attend(q_lat, q_pe, ckv, kpe, mask):
    s = (jnp.einsum('...qhr,...kr->...hqk', q_lat, ckv)
         + jnp.einsum('...qhp,...kp->...hqk', q_pe, kpe)).astype(jnp.float32) * ((C_NOPE + C_ROPE) ** -0.5)
    if mask is not None:
        s = jnp.where(mask, s, NEG)
    p = jax.nn.softmax(s, axis=-1).astype(ckv.dtype)
    return jnp.einsum('...hqk,...kr->...qhr', p, ckv)

def mla_prompt(q_lat, q_pe, ckv, kpe):
    B, S, H, R = q_lat.shape
    nb = S // MLA_Q_BLOCK
    kchunk = jnp.arange(S) // CHUNK

    def blk(args):
        i, ql, qp = args
        qchunk = (i * MLA_Q_BLOCK + jnp.arange(MLA_Q_BLOCK)) // CHUNK
        mask = (kchunk[None, :] <= qchunk[:, None])[None, None]
        return mla_attend(ql, qp, ckv, kpe, mask)

    def to_blocks(t):
        return jnp.swapaxes(t.reshape((B, nb, MLA_Q_BLOCK) + t.shape[2:]), 0, 1)

    o = lax.map(blk, (jnp.arange(nb), to_blocks(q_lat), to_blocks(q_pe)))
    return jnp.swapaxes(o, 0, 1).reshape(B, S, H, R)

def token_mix(z, pos, ws, bs, sink, g_q, w_uq, w_uk, w_uv, g_kv, cache):
    B, T = z.shape[:2]
    u, va, q, k, vb, cq, ckv_raw, kpe_raw = split_proj(z)
    q = rope(q.reshape(B, T, B_HEADS, B_HEAD_DIM), pos)
    k = rope(k.reshape(B, T, B_KV_HEADS, B_HEAD_DIM), pos)
    vb = vb.reshape(B, T, B_KV_HEADS, B_HEAD_DIM)
    qc = (rmsnorm(cq, g_q) @ w_uq).reshape(B, T, C_HEADS, C_NOPE + C_ROPE)
    q_nope, q_pe = qc[..., :C_NOPE], rope(qc[..., C_NOPE:], pos)
    q_lat = jnp.einsum('bthn,hrn->bthr', q_nope, w_uk)
    ckv = rmsnorm(ckv_raw, g_kv)
    kpe = rope(kpe_raw[:, :, None, :], pos)[:, :, 0, :]
    if cache is None:
        a = chunk_mlp_prompt(u, va, ws, bs)
        b = swa_prompt(q, k, vb, sink)
        c_lat = mla_prompt(q_lat, q_pe, ckv, kpe)
        w = min(WINDOW, T)
        state = (k[:, T - w:], vb[:, T - w:], ckv, kpe)
    else:
        ck, cv, cckv, ckpe = cache
        a = chunk_mlp_sample(u, va, ws, bs)
        b = swa_sample(q, k, vb, ck, cv, sink)
        c_lat = mla_attend(q_lat, q_pe, jnp.concatenate([cckv, ckv], axis=1),
                           jnp.concatenate([ckpe, kpe], axis=1), None)
        state = (k, vb, ckv, kpe, va)
    c = jnp.einsum('bthr,hrv->bthv', c_lat, w_uv).reshape(B, T, C_HEADS * C_V)
    return jnp.concatenate([a, b, c], axis=-1), state

def layer(h, pos, cache, n1, w1g, w1u, w1d, nm, w_in, ws, bs, sink, g_q, w_uq, w_uk, w_uv, g_kv,
          w_out, n2, w2g, w2u, w2d):
    h = ffn_half(h, n1, w1g, w1u, w1d)
    z = rmsnorm(h, nm) @ w_in
    m, st = token_mix(z, pos, ws, bs, sink, g_q, w_uq, w_uk, w_uv, g_kv, cache)
    h = h + m @ w_out
    h = ffn_half(h, n2, w2g, w2u, w2d)
    return h, st

def setup_inputs(seed: int = 0) -> dict:
    key = jax.random.key(seed)
    ks = iter(jax.random.split(key, 32))

    def nrm(shape, scale):
        return jax.random.normal(next(ks), shape, jnp.float32) * scale

    def gain(shape):
        return 1.0 + nrm(shape, 0.02)

    swa_c = min(WINDOW, PAST_LEN)
    return {
        "x_prompt": nrm((BATCH, SEQ, D_MODEL), 1.0),
        "x_sample": nrm((DEC_BATCH, DEC_SEQ, D_MODEL), 1.0),
        "cache_swa_k": nrm((DEPTH, DEC_BATCH, swa_c, B_KV_HEADS, B_HEAD_DIM), 1.0),
        "cache_swa_v": nrm((DEPTH, DEC_BATCH, swa_c, B_KV_HEADS, B_HEAD_DIM), 1.0),
        "cache_mla_ckv": nrm((DEPTH, DEC_BATCH, PAST_LEN, C_KV_LORA), 1.0),
        "cache_mla_kpe": nrm((DEPTH, DEC_BATCH, PAST_LEN, C_ROPE), 1.0),
        "norm_ffn1": gain((DEPTH, D_MODEL)),
        "w1_gate": nrm((DEPTH, D_MODEL, D_FF), D_MODEL ** -0.5),
        "w1_up": nrm((DEPTH, D_MODEL, D_FF), D_MODEL ** -0.5),
        "w1_down": nrm((DEPTH, D_FF, D_MODEL), D_FF ** -0.5),
        "norm_mix": gain((DEPTH, D_MODEL)),
        "w_in": nrm((DEPTH, D_MODEL, D_IN), D_MODEL ** -0.5),
        "cm_w_s": nrm((DEPTH, A_GROUPS, MLP_CHUNK, MLP_CHUNK), MLP_CHUNK ** -0.5),
        "cm_b": 1.0 + nrm((DEPTH, A_GROUPS, MLP_CHUNK), 0.1),
        "swa_sink": nrm((DEPTH, B_HEADS), 0.5),
        "mla_norm_q": gain((DEPTH, C_Q_LORA)),
        "mla_w_uq": nrm((DEPTH, C_Q_LORA, C_HEADS * (C_NOPE + C_ROPE)), C_Q_LORA ** -0.5),
        "mla_w_uk": nrm((DEPTH, C_HEADS, C_KV_LORA, C_NOPE), C_KV_LORA ** -0.5),
        "mla_w_uv": nrm((DEPTH, C_HEADS, C_KV_LORA, C_V), C_KV_LORA ** -0.5),
        "mla_norm_kv": gain((DEPTH, C_KV_LORA)),
        "w_out": nrm((DEPTH, D_MIX, D_MODEL), D_MIX ** -0.5),
        "norm_ffn2": gain((DEPTH, D_MODEL)),
        "w2_gate": nrm((DEPTH, D_MODEL, D_FF), D_MODEL ** -0.5),
        "w2_up": nrm((DEPTH, D_MODEL, D_FF), D_MODEL ** -0.5),
        "w2_down": nrm((DEPTH, D_FF, D_MODEL), D_FF ** -0.5),
        "norm_final": gain((D_MODEL,)),
    }

def reference(x_prompt, x_sample, cache_swa_k, cache_swa_v, cache_mla_ckv, cache_mla_kpe,
              norm_ffn1, w1_gate, w1_up, w1_down, norm_mix, w_in, cm_w_s, cm_b, swa_sink,
              mla_norm_q, mla_w_uq, mla_w_uk, mla_w_uv, mla_norm_kv, w_out,
              norm_ffn2, w2_gate, w2_up, w2_down, norm_final):
    S = x_prompt.shape[1]
    T = x_sample.shape[1]
    past = cache_mla_ckv.shape[2]
    pos_p = jnp.arange(S, dtype=jnp.int32)
    pos_s = past + jnp.arange(T, dtype=jnp.int32)
    hp, hs = x_prompt, x_sample
    st_p, st_s = [], []
    for l in range(DEPTH):
        wts = (norm_ffn1[l], w1_gate[l], w1_up[l], w1_down[l], norm_mix[l], w_in[l],
               cm_w_s[l], cm_b[l], swa_sink[l], mla_norm_q[l], mla_w_uq[l], mla_w_uk[l],
               mla_w_uv[l], mla_norm_kv[l], w_out[l], norm_ffn2[l], w2_gate[l], w2_up[l], w2_down[l])
        hp, sp = layer(hp, pos_p, None, *wts)
        hs, ss = layer(hs, pos_s, (cache_swa_k[l], cache_swa_v[l], cache_mla_ckv[l], cache_mla_kpe[l]), *wts)
        st_p.append(sp)
        st_s.append(ss)
    y_prompt = rmsnorm(hp, norm_final)
    y_sample = rmsnorm(hs, norm_final)
    swa_k_prompt = jnp.stack([s[0] for s in st_p])
    swa_v_prompt = jnp.stack([s[1] for s in st_p])
    mla_ckv_prompt = jnp.stack([s[2] for s in st_p])
    mla_kpe_prompt = jnp.stack([s[3] for s in st_p])
    swa_k_sample = jnp.stack([s[0] for s in st_s])
    swa_v_sample = jnp.stack([s[1] for s in st_s])
    mla_ckv_sample = jnp.stack([s[2] for s in st_s])
    mla_kpe_sample = jnp.stack([s[3] for s in st_s])
    chunkmlp_v_sample = jnp.stack([s[4] for s in st_s])
    return (y_prompt, y_sample, swa_k_prompt, swa_v_prompt, mla_ckv_prompt, mla_kpe_prompt,
            swa_k_sample, swa_v_sample, mla_ckv_sample, mla_kpe_sample, chunkmlp_v_sample)


_drawn_inputs = setup_inputs


def setup_inputs(seed=0):
    import zlib

    import numpy as np

    out = dict(_drawn_inputs(seed))
    spreads = {}
    factors = {'norm_ffn1': 4.591,
     'swa_sink': 64.0,
     'mla_norm_q': 8.0,
     'mla_norm_kv': 2.875,
     'norm_ffn2': 5.832,
     'norm_final': 7.832,
     'cache_swa_k': 4.142,
     'cache_swa_v': 3.46,
     'cache_mla_ckv': 6.667,
     'cache_mla_kpe': 8.0,
     'cm_b': 4.206}
    for name, (base, spread) in spreads.items():
        noise = np.random.default_rng([zlib.crc32(name.encode()), seed]).standard_normal(out[name].shape)
        drawn = base * np.exp(spread * noise) if base else spread * noise
        out[name] = __import__('jax').numpy.asarray(drawn.astype(out[name].dtype))
    for name, factor in factors.items():
        out[name] = (out[name] * factor).astype(out[name].dtype)
    return out
```

```python
from contextlib import ExitStack

import concourse.bass as bass
import numpy as np
from concourse import mybir

F32 = mybir.dt.float32
F32R = mybir.dt.float32r
ACT = mybir.ActivationFunctionType
ALU = mybir.AluOpType
AX_X = mybir.AxisListType.X

P = 128
D_MODEL, D_FF, DEPTH = 1024, 2816, 2
SEQ, DEC = 512, 64
NT = SEQ + DEC
HALF = NT // 2
KD = D_MODEL // P
KF = D_FF // P
CHUNK = 64
EPS = 1e-6
A_WIDTH, A_GROUPS, A_GDIM = 256, 4, 64
B_HEADS, B_KV_HEADS, B_DIM = 8, 2, 64
B_GROUP = B_HEADS // B_KV_HEADS
C_HEADS, C_Q, C_KV, C_NOPE, C_ROPE, C_V = 4, 384, 128, 64, 32, 64
KQ = C_Q // P
WINDOW, PAST = 128, 256
B_SCALE = float(B_DIM) ** -0.5
C_SCALE = float(C_NOPE + C_ROPE) ** -0.5
NEG = -1e30
COL_U, COL_VA, COL_Q, COL_K = 0, 256, 512, 1024
COL_V, COL_CQ, COL_CKV, COL_KPE = 1152, 1280, 1664, 1792
ROW_B, ROW_C = A_WIDTH, A_WIDTH + B_HEADS * B_DIM
TILES = [(t * P, min(P, NT - t * P)) for t in range(5)]

RAW, RING = 2, 4
SLOT = 8 * P
WIN = ["k", "v", "q0", "q1", "q2", "q3", "va0", "va1", "u0", "u1", "ckv", "cq0", "cq1", "cq2", "kpe", "qn"]
DOWN_TILES = [8, 8, 6]
F1G = 0
F1D = F1G + 2 * KF
ZIN = F1D + 3 * KD
AB = ZIN + len(WIN)
CC = AB + KD
F2G = CC + KD // 2
F2D = F2G + 2 * KF
SLOTS = F2D + 3 * KD
assert all(x % RING == 0 for x in (F1D, ZIN, AB, CC, F2G, F2D, SLOTS))


def slot_dmas(s):
    if AB <= s < CC:
        return 3
    if ZIN <= s < AB:
        return {"q": 2, "kpe": 1 + KQ, "qn": KQ}.get(WIN[s - ZIN][:1] if WIN[s - ZIN][0] == "q" and WIN[s - ZIN] != "qn" else WIN[s - ZIN], 1)
    return 1


def slot_size(s):
    if F1D <= s < ZIN or F2D <= s < SLOTS:
        return DOWN_TILES[(s - (F1D if s < ZIN else F2D)) % 3] * P
    if ZIN <= s < AB:
        return {"kpe": KD * C_ROPE + KQ * P, "qn": 2 * KQ * P}.get(WIN[s - ZIN], SLOT)
    if AB <= s < CC:
        return 6 * P
    if CC <= s < F2G:
        return 4 * P
    return SLOT


RAW_PER_LAYER = [sum(slot_dmas(s) for s in range(SLOTS) if s % RAW == r) for r in range(RAW)]


def raw_goal(layer, s, ahead):
    n = sum(slot_dmas(x) for x in range(s % RAW, s % SLOTS + 1, RAW))
    return (layer + s // SLOTS) * (16 * RAW_PER_LAYER[s % RAW]) + 16 * n + ahead * (16 // RAW)


UNITS = 2 * len(TILES)
MLA_TILES = [1, 3, 4, 2, 0]
MIX = """z:k sumx z:v tw z:q0 rot:k tv z:q1 rot:q0 tc z:q2 rot:q1 tk z:q3 rot:q2 z:va0 rot:q3 z:va1 tva:0
S:0 z:u0 tva:1 T:0 S:1 z:u1 a:0 T:1 O:0 S:2 z:ckv a:1 T:2 S:3 O:1 z:cq0 sumkv T:3 S:4 O:2 z:cq1
T:4 S:5 O:3 z:cq2 T:5 S:6 O:4 z:kpe tckv sumq T:6 rep S:7 O:5 qp rot:kpe T:7 S:8 qn:0 O:6 vc:0
T:8 tkpe vc:1 O:7 S:9 ql:1 rot:qp qn:1 ql:0 T:9 O:8 MS:0 ql:2 O:9 MT:0 ql:3 AB:0 MS:1 AB:1 MT:1
MS:2 MO:0 AB:2 MT:2 MS:3 MO:1 AB:3 MT:3 MS:4 MO:2 AB:4 MT:4 MS:5 MO:3 AB:5 MT:5 MO:4 MS:6 AB:6
MT:6 MS:7 MO:5 AB:7 MT:7 MS:8 MO:6 MT:8 MS:9 MO:7 MT:9 MO:8 MO:9""".split()


def split(step):
    kind, _, arg = step.partition(":")
    return kind, (int(arg) if arg.isdigit() else arg)


def swa_unit(n):
    i, g = n // 2, n % 2
    t0, nq = TILES[i]
    keys = [(-1, WINDOW), (4, DEC)] if i == 4 else ([(i - 1, P)] if i else []) + [(i, P)]
    return i, g, t0, nq, keys


def mla_unit(n):
    i, pair = MLA_TILES[n // 2], n % 2
    t0, nq = TILES[i]
    keys = [(-2, P), (-1, P), (4, DEC)] if i == 4 else [(t, P) for t in range(i + 1)]
    return i, pair, t0, nq, keys


def psum_pair(step):
    kind, arg = split(step)
    if kind in ("S", "MS"):
        return 1
    if kind in ("tw", "tv", "tc", "tk", "T", "MT"):
        return 2
    if kind in ("z", "qp", "qn", "AB"):
        return 1 if arg in ("v", "q1", "q3") else 0
    return 3


def scalar_ops(step):
    kind, arg = split(step)
    n = {"z": 0, "sumx": 1, "sumkv": 1, "sumq": 1, "tw": 2, "tv": 2, "tc": 2, "tk": 2, "tva": 2,
         "tckv": 2, "tkpe": 2, "rep": 1, "a": 1, "ql": 1, "S": 5, "O": 1, "MS": 2, "MO": 1}.get(kind, 0)
    if kind == "vc":
        n = 1 + arg
    if step == "z:ckv":
        n = 1
    if kind == "z" and arg.startswith("cq"):
        n = 2
    if kind == "T":
        n = 2 if swa_unit(arg)[0] == 4 else 1
    if kind == "MT":
        n = 2 if mla_unit(arg)[0] == 4 else 1
    return [f"{step}.{k}" for k in range(n)]


def vector_ops(step):
    kind, arg = split(step)
    n = {"z": 1, "sumx": 1, "sumkv": 2, "sumq": 1, "tw": 1, "rot": 3, "a": 4, "qp": 1, "qn": 1,
         "O": 1, "MO": 1, "AB": 1}.get(kind, 0)
    if kind == "z" and arg.startswith("cq"):
        n = 2 if arg == "cq0" else 3
    if kind == "S":
        n = 7 + (1 if swa_unit(arg)[0] in (0,) else 2 if swa_unit(arg)[0] < 4 else 0)
    if kind == "MS":
        n = 4 + (1 if mla_unit(arg)[0] < 4 else 0)
    return [f"{step}.{k}" for k in range(n)]


SLOT_ENDS = {("qp" if z == "kpe" else "qn:1" if z == "qn" else f"z:{z}"): ZIN + n for n, z in enumerate(WIN)}
SLOT_ENDS.update({f"AB:{m}": AB + m for m in range(KD)})
PE_STEPS = [s for s in MIX if s not in SLOT_ENDS]
ACT_STEPS = [x for s in MIX for x in scalar_ops(s)]
DVE_STEPS = [x for s in MIX for x in vector_ops(s)]


def evacuated(step):
    kind, arg = split(step)
    if kind in ("z", "qp", "qn", "O", "MO", "AB"):
        return "vector", f"{step}.0"
    if kind in ("rot", "a"):
        return "vector", f"{step}.1"
    return "scalar", scalar_ops(step)[-1]


def before_in_pair(step):
    at = MIX.index(step)
    same = [s for s in MIX[:at] if psum_pair(s) == psum_pair(step)]
    return same[-1] if same else None


def tensor_needs(step):
    kind, arg = split(step)
    prior = before_in_pair(step)
    scalar, vector = [], []
    if prior is not None:
        engine, name = evacuated(prior)
        (scalar if engine == "scalar" else vector).append(name)
    scalar += {
        "sumkv": lambda: ["z:ckv.0"],
        "rot": lambda: ["rep.0"] if arg == "kpe" else [],
        "a": lambda: [f"tva:{arg}.1"],
        "S": lambda: ["tc.1"] if arg == 0 else [],
        "MS": lambda: [f"ql:{2 * mla_unit(arg)[1] + 1}.0"],
        "O": lambda: [scalar_ops(f"T:{arg}")[-1]],
        "MO": lambda: [scalar_ops(f"MT:{arg}")[-1]],
        "vc": lambda: ["tc.0"],
    }.get(kind, list)()
    vector += {
        "sumq": lambda: ["z:cq2.2"],
        "rot": lambda: [] if arg == "kpe" else ["qp.0" if arg == "qp" else f"z:{arg}.0"],
        "rep": lambda: ["z:kpe.0"],
        "tv": lambda: ["z:v.0"],
        "tk": lambda: ["rot:k.2"],
        "tckv": lambda: ["sumkv.1"],
        "vc": lambda: ["sumkv.1"],
        "tkpe": lambda: ["rot:kpe.2"],
        "tva": lambda: [f"z:va{arg}.0"],
        "a": lambda: ["tw.0"],
        "qp": lambda: ["z:cq2.1"],
        "ql": lambda: [f"qn:{arg // 2}.0"],
        "S": lambda: ["rot:q3.2"] if arg == 0 else [],
        "MS": lambda: ["rot:qp.2"],
        "T": lambda: [vector_ops(f"S:{arg}")[-1]],
        "MT": lambda: [vector_ops(f"MS:{arg}")[-1]],
        "AB": lambda: ["a:1.3", f"O:{UNITS - 1}.0"] if arg == 0 else [],
    }.get(kind, list)()
    return scalar, vector


AHEAD = [0, 1, 2, 4]

G_FFN1, G_MIX, G_FFN2, G_Q, G_KV = 0, 24, 40, 56, 62
N_GAINS = 64


def build(nc, a, outs):
    ctx = ExitStack()
    with ctx:
        def at(name, shape, dtype, offset):
            return nc.alloc_sbuf_tensor_at(name, shape, dtype, offset=offset)

        def sb(name, shape, dtype=F32):
            return ctx.enter_context(nc.sbuf_tensor(name, shape, dtype))

        U = NT * 4
        ACT_BYTES, X_BYTES, TEMP_BYTES = 2 * KF * U, 2 * KD * U, 2 * U
        arena_len = ACT_BYTES + X_BYTES + TEMP_BYTES
        arena0 = (nc.sbuf_base + 31) // 32 * 32
        sb("arena", [P, arena_len // 4])
        act0, x0, temp0 = arena0, arena0 + ACT_BYTES, arena0 + ACT_BYTES + X_BYTES

        h = sb("h", [P, KD, NT])
        raw = [sb(f"raw{r}", [P, SLOT]) for r in range(RAW)]
        wh = [sb(f"w_high{r}", [P, SLOT], F32R) for r in range(RING)]
        wl = [sb(f"w_low{r}", [P, SLOT], F32R) for r in range(RING)]
        rms = sb("rms", [P, NT])
        sq_sum = sb("sq_sum", [P, NT])
        sq_tmp = sb("sq_tmp", [P, NT])
        ident = sb("ident", [P, P])
        root_tok = sb("root_tok", [P, 5])
        rot64 = sb("rot64", [P, P])
        rep32 = sb("rep32", [C_ROPE, P])
        mean_d = sb("mean_d", [P, P])
        gains = sb("gains", [P, N_GAINS])
        eps = sb("eps", [P, 1])
        sinks = sb("sinks", [P, B_HEADS])
        neg_sink = sb("neg_sink", [P, B_HEADS])
        top = sb("top", [P, 4])
        neg_max = sb("neg_max", [P, 4])
        sink_arg = sb("sink_arg", [P, 4])
        sink_exp = sb("sink_exp", [P, 4])
        den = sb("den", [P, 4])
        den_all = sb("den_all", [P, 4])
        inv_den = sb("inv_den", [P, 4])

        xh = at("x_high", [P, KD, NT], F32R, x0)
        xl = at("x_low", [P, KD, NT], F32R, x0 + KD * U)
        fh = at("hidden_high", [P, KF, NT], F32R, act0)
        fl = at("hidden_low", [P, KF, NT], F32R, act0 + KF * U)
        gate = at("gate", [P, NT], F32, temp0)
        up = at("up", [P, NT], F32, temp0 + U)

        cursor = [act0]

        def mix(name, shape, dtype=F32):
            t = at(name, shape, dtype, cursor[0])
            cursor[0] += (int(np.prod(shape[1:])) * 4 + 31) // 32 * 32
            return t

        mh = mix("mixed_high", [P, KD, NT], F32R)
        ml = mix("mixed_low", [P, KD, NT], F32R)
        qT = [mix(f"qT{j}", [P, NT]) for j in range(4)]
        kT = mix("kT", [P, NT])
        zs = [mix(f"z{j}", [P, NT]) for j in range(2)]
        ckvT = mix("ckvT", [P, NT])
        cq_at = cursor[0]
        cos64 = mix("cos64", [P, NT])
        sin64 = mix("sin64", [P, NT])
        vT = mix("vT", [P, NT])
        uT = [mix(f"uT{j}", [P, NT]) for j in range(2)]
        cursor[0] += U
        cqh = at("cq_high", [P, KQ, NT], F32R, cq_at)
        cql = at("cq_low", [P, KQ, NT], F32R, cq_at + KQ * U)
        probs_at = cursor[0]
        probs = mix("probs", [P, 1024])
        pT0_at = cursor[0]
        probsT = [mix(f"probsT{j}", [P, 1024]) for j in range(2)]
        ws = at("w_s", [P, A_GROUPS, P], F32, pT0_at)
        wuk = at("w_uk", [P, C_HEADS, C_NOPE], F32, pT0_at + 2048)
        ck = at("cache_k", [P, P], F32, pT0_at + 3072)
        ckpe4 = at("cache_kpe4", [P, 2, 4, C_ROPE], F32, pT0_at + 4096)
        va_tok = mix("va_tok", [P, 5, A_WIDTH])
        v_tok = mix("v_tok", [P, 5, P])
        k_tok = sb("k_tok", [P, 2, P])
        ckv_tok = mix("ckv_tok", [P, 5, P])
        wukT = mix("w_ukT", [P, 2, P])
        wuv = mix("w_uv", [P, C_HEADS, C_V])
        wsT = mix("w_sT", [P, A_GROUPS, P])
        bias_a = mix("bias_a", [P, 2, P])
        cv = mix("cache_v", [P, P])
        cckv = mix("cache_ckv", [P, 2, P])
        cT = mix("cache_kT_ckvT", [P, 3 * P])
        ckpeT = mix("cache_kpeT", [P, 2 * P])
        assert cursor[0] <= x0, cursor[0] - x0
        work = at("work", [P, NT], F32, temp0)
        squares = at("squares", [P, KD, NT], F32, act0 + 2 * KD * U)
        rms_kv = at("rms_kv", [P, NT], F32, temp0 + U)
        cursor[0] = x0
        qlT = [mix(f"q_latT{j}", [P, NT]) for j in range(C_HEADS)]
        qnT = [mix(f"q_nopeT{j}", [P, NT]) for j in range(2)]
        qpT = mix("q_peT", [P, NT])
        kpeT = mix("kpeT", [P, NT])
        kpe_rep = mix("kpe_rep", [P, NT])
        rms_q = mix("rms_q", [P, NT])
        rot32 = mix("rot32", [P, P])
        cos32 = mix("cos32", [P, NT])
        sin32 = mix("sin32", [P, NT])
        vc_tok = mix("vc_tok", [P, 7, C_HEADS * C_V])
        kpe_tok = mix("kpe_tok", [P, 5, C_ROPE])
        assert cursor[0] <= temp0
        x_tok = at("x_tok", [P, 5, D_MODEL], F32, act0)
        g_rows = at("gain_rows", [N_GAINS, P], F32, act0 + 5 * D_MODEL * 4)
        y_tok = at("y_tok", [P, 5, D_MODEL], F32, act0)
        ident_r = at("ident_r", [P, P], F32R, temp0 + U)

        ps = [ctx.enter_context(nc.psum_tensor(f"pair{p}", [P, 2, 512], F32)) for p in range(4)]

        def halves(p):
            return ps[p][:, :, 0:HALF]

        def two(t):
            return t.rearrange("p (a n) -> p a n", a=2)

        def flat(p):
            return ps[p][:, :, :].rearrange("p a n -> p (a n)")

        def sem(name):
            return ctx.enter_context(nc.semaphore(name))

        waits_passed = sem("waits_passed")
        raw_loaded = [sem(f"raw_loaded{r}") for r in range(RAW)]
        high_ready, low_ready, slot_used = sem("high_ready"), sem("low_ready"), sem("slot_used")
        ident_in, consts_in, gain_rows_in = sem("ident_in"), sem("consts_in"), sem("gain_rows_in")
        x_in = [sem(f"x_in{f}") for f in range(2)]
        const_made, gains_T, gains_ready = sem("const_made"), sem("gains_transposed"), sem("gains_ready")
        xT_done = sem("xT_done")
        h_ready, xh_ready, x_ready = sem("h_ready"), sem("xh_ready"), sem("x_ready")
        sq_made, sq_added = sem("sq_made"), sem("sq_added")
        sum_done, root_done, rms_ready = sem("sum_done"), sem("root_done"), sem("rms_ready")
        up_scaled = sem("up_scaled")
        g_scaled, silu_done, prod_ready = sem("g_scaled"), sem("silu_done"), sem("prod_ready")
        fh_ready, f_ready = sem("hidden_high_ready"), sem("hidden_ready")
        c_even_done = sem("c_even_done")
        cleared = sem("sq_sum_cleared")
        pe_step, act_step, dve_step = sem("pe_step"), sem("act_step"), sem("dve_step")
        mix_in, table_in, mix_stored = sem("mix_in"), sem("table_in"), sem("mix_stored")
        y_done, y_stored, y_scale = sem("y_done"), sem("y_stored"), sem("y_scale")
        ident_made = sem("ident_made")
        y_left, y_right = sem("y_left"), sem("y_right")
        h_part = sem("h_sample_part")

        def stand_alone(eng):
            eng.sem_inc(waits_passed, 1)

        def slot_done(eng, layer, s, ahead=0):
            eng.wait_ge(slot_used, layer * SLOTS + ahead + (RING + s + 1))

        def pe_did(eng, layer, name):
            if name in SLOT_ENDS:
                slot_done(eng, layer, SLOT_ENDS[name])
            else:
                eng.wait_ge(pe_step, layer * len(PE_STEPS) + (PE_STEPS.index(name) + 1))

        def act_did(eng, layer, name):
            eng.wait_ge(act_step, layer * len(ACT_STEPS) + (ACT_STEPS.index(name) + 1))

        def dve_did(eng, layer, name):
            eng.wait_ge(dve_step, layer * len(DVE_STEPS) + (DVE_STEPS.index(name) + 1))

        def updates(layer, phase):
            return KD + layer * (3 * KD) + KD * phase

        MIX_IN_FIRST = 16 * 17
        N_MIX_IN = MIX_IN_FIRST + 16 * 3
        N_STORES = 9

        block = ctx.enter_context(nc.Block())

        @block.sync
        def _(sp):
            sp.dma_start(ident[:, :], a["const"][0]).then_inc(ident_in, 16)
            for row, name in ((0, "norm_ffn1"), (G_MIX, "norm_mix"), (G_FFN2, "norm_ffn2"),
                              (G_Q, "mla_norm_q"), (G_KV, "mla_norm_kv")):
                src = a[name].rearrange("l (m p) -> (l m) p", p=P)
                sp.dma_start(g_rows[row:row + src.shape[0], :], src).then_inc(gain_rows_in, 16)
            sp.dma_start(g_rows[2 * KD:3 * KD, :], a["norm_final"].rearrange("(m p) -> m p", p=P)).then_inc(gain_rows_in, 16)

            sp.dma_start(mean_d[:, :], a["const"][3]).then_inc(consts_in, 16)
            sp.dma_start(rot64[:, :], a["const"][1]).then_inc(consts_in, 16)
            sp.dma_start(rep32[:, :], a["const"][4, 0:C_ROPE]).then_inc(consts_in, 16)

            def into(s, layer, ahead, pairs):
                sp.wait_ge(low_ready, layer * SLOTS + ahead + (s + 1))
                stand_alone(sp)
                assert len(pairs) == slot_dmas(s)
                for dst, src in pairs:
                    sp.dma_start(dst, src).then_inc(raw_loaded[s % RAW], 16)

            def tiles(s, n, k0=0):
                return raw[s % RAW][:, k0 * P:(k0 + n) * P].rearrange("p (k c) -> p k c", c=P)

            def gate_up(layer, base_slot, w_up, w_gate):
                with sp.Fori(0, KF // 2) as i:
                    for r in range(4):
                        w = (w_up, w_gate)[r % 2]
                        src = w[layer].rearrange("(k p) n -> p k n", p=P)[:, :, bass.ds((2 * i + r // 2) * P, P)]
                        into(base_slot + r, layer, 4 * i, [(tiles(r, KD), src)])

            def down(layer, base_slot, w):
                with sp.Fori(0, KD // 4) as i:
                    for r in range(12):
                        k0, n = 8 * (r % 3), DOWN_TILES[r % 3]
                        src = w[layer, k0 * P:(k0 + n) * P, :].rearrange("(k p) n -> p k n", p=P)[:, :, bass.ds((4 * i + r // 3) * P, P)]
                        into(base_slot + r, layer, 12 * i, [(tiles(r, n), src)])

            def w_in(layer):
                src = a["w_in"][layer].rearrange("(k p) n -> p k n", p=P)
                for n, z in enumerate(WIN):
                    s = ZIN + n
                    if z[0] == "q" and z != "qn":
                        j = int(z[1])
                        pairs = [(tiles(s, KD)[:, :, g * 64:g * 64 + 64],
                                  src[:, :, COL_Q + (g * B_GROUP + j) * B_DIM:COL_Q + (g * B_GROUP + j + 1) * B_DIM])
                                 for g in range(2)]
                    elif z in ("kpe", "qn"):
                        uq = a["mla_w_uq"][layer].rearrange("(k p) (h n) -> p k h n", p=P, n=C_NOPE + C_ROPE)
                        r = raw[s % RAW]
                        if z == "kpe":
                            pairs = [(r[:, 0:KD * C_ROPE].rearrange("p (k c) -> p k c", c=C_ROPE), src[:, :, COL_KPE:COL_KPE + C_ROPE])]
                            pairs += [(r[:, KD * C_ROPE + k * P:KD * C_ROPE + (k + 1) * P].rearrange("p (h n) -> p h n", h=C_HEADS),
                                       uq[:, k, :, C_NOPE:]) for k in range(KQ)]
                        else:
                            pairs = [(r[:, k * 2 * P:(k + 1) * 2 * P].rearrange("p (h n) -> p h n", h=C_HEADS),
                                      uq[:, k, :, 0:C_NOPE]) for k in range(KQ)]
                    else:
                        col = {"k": COL_K, "v": COL_V, "ckv": COL_CKV}.get(z)
                        if col is None:
                            col = {"va": COL_VA, "u": COL_U, "cq": COL_CQ}[z[:-1]] + int(z[-1]) * P
                        pairs = [(tiles(s, KD), src[:, :, col:col + P])]
                    into(s, layer, 0, pairs)
                    if n == 3:
                        mix_loads(layer)

            def mix_loads(layer):
                sp.wait_ge(slot_used, layer * SLOTS + (RING + ZIN))
                stand_alone(sp)
                def load(dst, src):
                    count[0] += 1
                    sp.dma_start(dst, src).then_inc(mix_in, 16)
                count = [0]
                load(cos64[:, :], a["rope"][0])
                load(sin64[:, :], a["rope"][1])
                load(wuk[:, :, :], a["mla_w_uk"][layer].rearrange("h r n -> r h n"))
                load(ws[:, :, :], a["cm_w_s"][layer].rearrange("g i j -> i g j"))
                load(ck[:, :], a["cache_swa_k"][layer, 0].rearrange("t h d -> t (h d)"))
                load(cv[:, :], a["cache_swa_v"][layer, 0].rearrange("t h d -> t (h d)"))
                load(cckv[:, :, :], a["cache_mla_ckv"][layer, 0].rearrange("(b t) r -> t b r", t=P))
                for c in range(4):
                    load(ckpe4[:, :, c, :], a["cache_mla_kpe"][layer, 0].rearrange("(b t) r -> t b r", t=P))
                load(wuv[:, :, :], a["mla_w_uv"][layer].rearrange("h r v -> r h v"))
                for g in range(A_GROUPS):
                    r = 64 * (g % 2)
                    load(bias_a[r:r + 64, g // 2, :], a["cm_b"][layer, g].partition_broadcast(64))
                load(sinks[:, :], a["swa_sink"][layer].partition_broadcast(P))
                assert 16 * count[0] == MIX_IN_FIRST

            def stores(layer):
                def store(dst, src):
                    sp.dma_start(dst, src).then_inc(mix_stored, 16)
                for name in ("tk.1", "tv.1", "tckv.1", "tkpe.1", "tva:1.1"):
                    act_did(sp, layer, name)
                    stand_alone(sp)
                o = outs
                store(o[2][layer, 0].rearrange("t h d -> t (h d)"), k_tok[:, 0, :])
                store(o[3][layer, 0].rearrange("t h d -> t (h d)"), v_tok[:, 3, :])
                store(o[4][layer, 0].rearrange("(b t) r -> t b r", t=P), ckv_tok[:, 0:4, :])
                store(o[5][layer, 0].rearrange("(b t) r -> t b r", t=P), kpe_tok[:, 0:4, :])
                store(o[6][layer, 0].rearrange("t h d -> t (h d)"), k_tok[0:DEC, 1, :])
                store(o[7][layer, 0].rearrange("t h d -> t (h d)"), v_tok[0:DEC, 4, :])
                store(o[8][layer, 0], ckv_tok[0:DEC, 4, :])
                store(o[9][layer, 0], kpe_tok[0:DEC, 4, :])
                store(o[10][layer, 0], va_tok[0:DEC, 4, :])

            def w_out(layer):
                w = a["w_out"][layer]
                for m in range(KD):
                    s = AB + m
                    c = slice(m * P, (m + 1) * P)
                    pairs = [(tiles(s, 2), w[0:ROW_B, c].rearrange("(k p) n -> p k n", p=P))]
                    for g in range(2):
                        r0 = ROW_B + g * B_GROUP * B_DIM
                        pairs.append((tiles(s, 4, 2)[g * 64:g * 64 + 64],
                                      w[r0:r0 + B_GROUP * B_DIM, c].rearrange("(j d) n -> d j n", d=B_DIM)))
                    into(s, layer, 0, pairs)
                    if m == 3:
                        stores(layer)
                for c in range(KD // 2):
                    dst = raw[c % RAW][:, 0:4 * P].rearrange("p (k c) -> p k c", k=2)
                    into(CC + c, layer, 0, [(dst, w[ROW_C:, c * 2 * P:(c + 1) * 2 * P].rearrange("(k p) n -> p k n", p=P))])

            with sp.Fori(0, DEPTH) as layer:
                gate_up(layer, F1G, a["w1_up"], a["w1_gate"])
                down(layer, F1D, a["w1_down"])
                w_in(layer)
                w_out(layer)
                gate_up(layer, F2G, a["w2_up"], a["w2_gate"])
                down(layer, F2D, a["w2_down"])
            for r in range(2):
                sp.wait_ge(low_ready, DEPTH * SLOTS + r + 1)
                sp.dma_start(tiles(r, KD), a["w1_up"][0].rearrange("(k p) n -> p k n", p=P)[:, :, 0:P]).then_inc(raw_loaded[r], 16)
            for t, (t0, n) in enumerate(TILES):
                sp.wait_ge(y_left, t + 1)
                sp.wait_ge(y_right, t + 1)
                dst = outs[0][0, t0:t0 + n, :] if t < 4 else outs[1][0]
                sp.dma_start(dst, y_tok[0:n, t, :]).then_inc(y_stored, 16)
            sp.wait_ge(mix_stored, 16 * N_STORES * DEPTH)
            sp.wait_ge(y_stored, 16 * len(TILES))

        @block.gpsimd
        def _(pool):
            pool.sem_inc(low_ready, RAW)
            low_of = lambda r, n: dict(out=wl[r % RING][:, 0:n], in0=raw[r % RAW][:, 0:n],
                                       in1=wh[r % RING][:, 0:n].bitcast(F32), op=ALU.subtract)

            def low(layer, s, ahead):
                pool.wait_ge(high_ready, layer * SLOTS + ahead + (s + 1))
                nc.gpsimd.tensor_tensor(**low_of(s, slot_size(s))).then_inc(low_ready, 1)

            def ffn(layer, g, d):
                with pool.Fori(0, KF // 2) as i:
                    for r in range(4):
                        low(layer, g + r, 4 * i)
                with pool.Fori(0, KD // 4) as i:
                    for r in range(12):
                        low(layer, d + r, 12 * i)

            with pool.Fori(0, DEPTH) as layer:
                ffn(layer, F1G, F1D)
                for s in range(ZIN, F2G):
                    low(layer, s, 0)
                ffn(layer, F2G, F2D)

        @block.scalar
        def _(act):
            def high(layer, s, ahead=0):
                act.wait_ge(raw_loaded[s % RAW], raw_goal(layer, s, ahead))
                act.wait_ge(slot_used, layer * SLOTS + ahead + (s + 1))
                n = slot_size(s % SLOTS)
                nc.scalar.activation(wh[s % RING][:, 0:n], raw[s % RAW][:, 0:n], ACT.Copy).then_inc(high_ready, 1)

            def gain_at(col):
                return gains[:, col:col + 1] if isinstance(col, int) else gains[:, bass.ds(col, 1)]

            def absorb_all(count, gain_col, ahead, late):
                def square(m):
                    nc.scalar.activation(squares[:, m, :], h[:, m, :], ACT.Square).then_inc(sq_made, 1)
                for m in range(KD):
                    ahead(m)
                    act.wait_ge(h_ready, count + (m + 1))
                    nc.scalar.activation(xh[:, m, :], h[:, m, :], ACT.Copy, scale=gain_at(gain_col + m)).then_inc(xh_ready, 1)
                    if m >= late:
                        square(m - late)
                for m in range(KD - late, KD):
                    square(m)

            def absorb(m, count, gain_col):
                act.wait_ge(h_ready, count + 1)
                nc.scalar.activation(xh[:, m, :], h[:, m, :], ACT.Copy, scale=gain_at(gain_col)).then_inc(xh_ready, 1)
                act.wait_ge(sq_added, count + 1)
                stand_alone(act)
                nc.scalar.activation(sq_tmp[:, :], h[:, m, :], ACT.Square).then_inc(sq_made, 1)

            def root(count):
                act.wait_ge(sum_done, count + 1)
                nc.scalar.activation(two(rms[:, :]), halves(3), ACT.Sqrt, bias=eps[:, 0:1]).then_inc(root_done, 1)

            def gate_up(layer, w, base_slot):
                def chunk(i, r, first=False):
                    c = layer * (2 * KF) + 2 * i + (w * KF + r)
                    high(layer, base_slot + 2 * r + 2, 4 * i)
                    high(layer, base_slot + 2 * r + 3, 4 * i)
                    if first:
                        root(2 * layer + w)
                    act.wait_ge(g_scaled, c + 1)
                    nc.scalar.activation(gate[:, :], gate[:, :], ACT.Silu).then_inc(silu_done, 1)
                    act.wait_ge(prod_ready, c + 1)
                    nc.scalar.activation(fh[:, bass.ds(2 * i + r, 1), :], gate[:, :].unsqueeze(1), ACT.Copy).then_inc(fh_ready, 1)
                chunk(0, 0, first=True)
                chunk(0, 1)
                with act.Fori(1, KF // 2) as i:
                    for r in range(2):
                        chunk(i, r)

            def down(layer, base_slot, phase, gain_base):
                with act.Fori(0, KD // 4) as i:
                    for r in range(4):
                        for k in range(3):
                            high(layer, base_slot + 3 * r + k + 2, 12 * i)
                        absorb(bass.ds(4 * i + r, 1), updates(layer, phase) + 4 * i + r, gain_base + 4 * i + r)

            def mixing(layer):
                def did(name):
                    pe_did(act, layer, name)

                def emit(ins, name):
                    assert ACT_STEPS[emitted[0]] == name, (ACT_STEPS[emitted[0]], name)
                    emitted[0] += 1
                    ins.then_inc(act_step, 1)
                emitted = [0]

                def copy(out, src, name, **kw):
                    emit(nc.scalar.activation(out, src, ACT.Copy, **kw), name)

                def tok_copies(step, dst, src_w):
                    p = psum_pair(step)
                    copy(dst[:, 0:4, :], ps[p][:, 0, 0:4 * src_w].rearrange("p (t c) -> p t c", t=4), f"{step}.0")
                    copy(dst[0:DEC, 4, :], ps[p][0:DEC, 1, 0:src_w], f"{step}.1")

                slot = [ZIN]
                for step in MIX:
                    kind, arg = split(step)
                    p = psum_pair(step)
                    if kind in ("z", "AB") or step == "qn:0":
                        high(layer, slot[0] + 2)
                        slot[0] += 1
                    if not scalar_ops(step):
                        if step == "z:kpe":
                            did("z:kpe")
                            act.dma_start(cos32[:, :], a["rope"][2]).then_inc(mix_in, 16)
                            act.dma_start(sin32[:, :], a["rope"][3]).then_inc(mix_in, 16)
                            act.dma_start(rot32[:, :], a["const"][2]).then_inc(mix_in, 16)
                        continue
                    if kind == "z":
                        dve_did(act, layer, f"{step}.0")
                        if arg == "ckv":
                            emit(nc.scalar.activation(sq_sum[:, :], ckvT[:, :], ACT.Square), "z:ckv.0")
                        else:
                            c = int(arg[2:])
                            dst = sq_tmp if c == 0 else sq_sum
                            src = zs[1 if c != 1 else 0]
                            emit(nc.scalar.activation(dst[:, :], src[:, :], ACT.Square), f"{step}.0")
                            copy(cqh[:, c, :], src[:, :], f"{step}.1", scale=gains[:, bass.ds(layer * KQ + (G_Q + c), 1)])
                        continue
                    if kind == "a":
                        dve_did(act, layer, f"{step}.2")
                        copy(mh[:, arg, :], work[:, :], f"{step}.0")
                        continue
                    did(step)
                    if kind.startswith("sum"):
                        dst, width = {"sumx": (rms, D_MODEL), "sumkv": (rms_kv, C_KV), "sumq": (rms_q, C_Q)}[kind]
                        emit(nc.scalar.activation(two(dst[:, :]), halves(p), ACT.Sqrt, bias=eps[:, 0:1],
                                                  scale=D_MODEL / width), f"{step}.0")
                    elif kind == "tw":
                        copy(wukT[:, :, :], ps[p][:, 0, 0:2 * P].rearrange("p (b r) -> p b r", b=2), "tw.0")
                        copy(wsT[:, :, :], ps[p][:, 1, :].rearrange("p (g i) -> p g i", g=A_GROUPS), "tw.1")
                    elif kind == "tc":
                        copy(cT[:, :], ps[p][:, 0, 0:3 * P], "tc.0")
                        copy(ckpeT[:, :], ps[p][:, 1, 0:2 * P], "tc.1")
                    elif kind == "tk":
                        copy(k_tok[:, 0, :], ps[p][:, 0, 0:P], "tk.0")
                        copy(k_tok[0:DEC, 1, :], ps[p][0:DEC, 1, 0:P], "tk.1")
                    elif kind == "tv":
                        tok_copies(step, v_tok, P)
                    elif kind == "tckv":
                        tok_copies(step, ckv_tok, P)
                    elif kind == "tkpe":
                        tok_copies(step, kpe_tok, C_ROPE)
                    elif kind == "tva":
                        tok_copies(step, va_tok[:, :, arg * P:(arg + 1) * P], P)
                    elif kind == "rep":
                        copy(two(kpe_rep[:, :]), halves(p), "rep.0")
                    elif kind == "ql":
                        copy(two(qlT[arg][:, :]), halves(p), f"{step}.0")
                    elif kind == "S":
                        i, g, t0, nq, keys = swa_unit(arg)
                        W = sum(n for _, n in keys)
                        first = len(vector_ops(step)) - 7
                        dve_did(act, layer, f"{step}.{first + 2}")
                        emit(nc.scalar.activation(sink_exp[0:nq, :], sink_arg[0:nq, :], ACT.Exp), f"{step}.0")
                        for j in range(B_GROUP):
                            emit(nc.scalar.activation(probs[0:nq, j * 256:j * 256 + W], flat(p)[0:nq, j * 256:j * 256 + W],
                                                      ACT.Exp, bias=neg_max[0:nq, j:j + 1], scale=B_SCALE,
                                                      accum_out=den[0:nq, j:j + 1]), f"{step}.{1 + j}")
                    elif kind == "MS":
                        i, pair, t0, nq, keys = mla_unit(arg)
                        W = sum(n for _, n in keys)
                        dve_did(act, layer, f"{step}.{len(vector_ops(step)) - 3}")
                        for j in range(2):
                            emit(nc.scalar.activation(probs[0:nq, j * 512:j * 512 + W], flat(p)[0:nq, j * 512:j * 512 + W],
                                                      ACT.Exp, bias=neg_max[0:nq, j:j + 1], scale=C_SCALE,
                                                      accum_out=den[0:nq, j:j + 1]), f"{step}.{j}")
                    elif kind in ("T", "MT"):
                        i, _, t0, nq, keys = (swa_unit if kind == "T" else mla_unit)(arg)
                        dst = probsT[arg % 2]
                        w = 512 if kind == "T" else 2 * nq
                        used = 4 * nq if kind == "T" else 2 * nq
                        if i != 4:
                            copy(dst[:, 0:len(keys) * w], flat(p)[:, 0:len(keys) * w], f"{step}.0")
                        else:
                            full = len(keys) - 1
                            src = flat(p)[:, 0:full * w].rearrange("p (k c) -> p k c", k=full)[:, :, 0:used]
                            copy(dst[:, 0:full * w].rearrange("p (k c) -> p k c", k=full)[:, :, 0:used], src, f"{step}.0")
                            copy(dst[0:DEC, full * w:full * w + used], flat(p)[0:DEC, full * w:full * w + used], f"{step}.1")
                    elif kind == "O":
                        i, g, t0, nq, keys = swa_unit(arg)
                        r = slice(64 * g, 64 * g + 64)
                        copy(mh[r, 2:6, t0:t0 + nq], ps[p][r, 0, 0:4 * nq].rearrange("p (j n) -> p j n", j=4), f"{step}.0")
                    elif kind == "vc":
                        if arg == 0:
                            copy(vc_tok[:, 0:4, :], flat(p).rearrange("p (t c) -> p t c", t=4), "vc:0.0")
                        else:
                            copy(vc_tok[:, 4:6, :], ps[p][:, 0, :].rearrange("p (t c) -> p t c", t=2), "vc:1.0")
                            copy(vc_tok[0:DEC, 6, :], ps[p][0:DEC, 1, 0:C_HEADS * C_V], "vc:1.1")
                    elif kind == "MO":
                        i, pair, t0, nq, keys = mla_unit(arg)
                        copy(mh[:, 6 + pair, t0:t0 + nq], ps[p][:, 0, 0:nq], f"{step}.0")
                assert emitted[0] == len(ACT_STEPS)

            for f in range(2):
                c = slice(f * (D_MODEL // 2), (f + 1) * (D_MODEL // 2))
                act.dma_start(x_tok[:, 0:4, c], a["x_prompt"][0].rearrange("(t p) d -> p t d", p=P)[:, :, c]).then_inc(x_in[f], 16)
                act.dma_start(x_tok[0:DEC, 4, c], a["x_sample"][0, :, c]).then_inc(x_in[f], 16)
            def sample_part(m):
                act.wait_ge(xT_done, m + 1)
                nc.scalar.activation(h[:, m, SEQ:NT], ps[m % 4][:, 1, 0:DEC], ACT.Copy).then_inc(h_part, 1)

            def ahead_of_first(m):
                if 2 <= m + 1 < KD:
                    sample_part(m + 1)
                if m in (1, 2):
                    high(0, m - 1)
            sample_part(0)
            sample_part(1)
            act.wait_ge(gains_T, 1)
            nc.scalar.activation(gains[:, :], ps[3][:, 1, 0:N_GAINS], ACT.Copy).then_inc(gains_ready, 1)
            act.wait_ge(gains_ready, 1)
            act.wait_ge(const_made, 3)
            absorb_all(0, 0, ahead_of_first, 6)

            with act.Fori(0, DEPTH) as layer:
                gate_up(layer, 0, F1G)
                down(layer, F1D, 0, layer * KD + G_MIX)
                mixing(layer)
                act.wait_ge(mix_stored, (layer + 1) * (16 * N_STORES))
                def ahead(m):
                    if m in AHEAD:
                        high(layer, CC + 2 + AHEAD.index(m))
                absorb_all(updates(layer, 1), layer * KD + G_FFN2, ahead, 2)
                gate_up(layer, 1, F2G)
                down(layer, F2D, 2, layer * KD + (G_FFN1 + KD))
            act.wait_ge(sum_done, 2 * DEPTH + 1)
            nc.scalar.activation(root_tok[:, 0:4], ps[3][:, 0, 0:4], ACT.Sqrt, bias=eps[:, 0:1]).then_inc(root_done, 1)
            nc.scalar.activation(root_tok[0:DEC, 4:5], ps[3][0:DEC, 0, 4:5], ACT.Sqrt, bias=eps[0:DEC, 0:1]).then_inc(root_done, 1)
            act.wait_ge(y_scale, 1)
            for t, (t0, n) in enumerate(TILES):
                act.wait_ge(y_done, t + 1)
                nc.scalar.activation(y_tok[0:n, t, 0:512], ps[t % 4][0:n, 0, :], ACT.Copy, scale=root_tok[0:n, t:t + 1]).then_inc(y_left, 1)

        @block.tensor
        def _(pe):
            pe.sem_inc(slot_used, RING)

            def product(p, tiles3, first=True, last=True, before=None):
                n = len(tiles3)
                for k, (w_h, w_l, x_h, x_l) in enumerate(tiles3):
                    if before is not None:
                        before(k)
                    for q, (w, x) in enumerate(((w_h, x_h), (w_h, x_l), (w_l, x_h))):
                        for half in range(2):
                            mm = nc.tensor.matmul(ps[p][:, half, 0:HALF], w, x[:, half * HALF:(half + 1) * HALF],
                                                  start=first and k == 0 and q == 0, stop=last and k == n - 1 and q == 2)
                return mm

            def low_in(layer, s, ahead=0):
                pe.wait_ge(low_ready, layer * SLOTS + ahead + (s + 1 + RAW))

            def tile_w(s, k, off=0):
                c = slice(off + k * P, off + (k + 1) * P)
                return wh[s % RING][:, c], wl[s % RING][:, c]

            def x_tiles(s):
                return [(*tile_w(s, k), xh[:, k, :], xl[:, k, :]) for k in range(KD)]

            def mean_of(src, p=3):
                for half in range(2):
                    mm = nc.tensor.matmul(ps[p][:, half, 0:HALF], mean_d[:, :], src[:, half * HALF:(half + 1) * HALF], start=True, stop=True)
                return mm

            def gate_up(layer, w, base_slot, x_count):
                def chunk(i, r):
                    c = layer * (2 * KF) + 2 * i + (w * KF + r)
                    s = base_slot + 2 * r
                    if not (isinstance(i, int) and i == 0):
                        pe.wait_ge(g_scaled, c - 1)
                    low_in(layer, s, 4 * i)
                    release(product(2 * r, x_tiles(s)))
                    low_in(layer, s + 1, 4 * i)
                    if isinstance(i, int) and i == 0 and r == 1:
                        pe.wait_ge(root_done, 2 * layer + (w + 1))
                    release(product(2 * r + 1, x_tiles(s + 1)))

                low_in(layer, base_slot + 1)
                pe.wait_ge(h_ready, x_count + 6)
                for k in range(KD):
                    pe.wait_ge(x_ready, x_count + (k + 1))
                    for r in range(2):
                        mm = product(r, [x_tiles(base_slot + r)[k]], first=k == 0, last=k == KD - 1)
                        if k == KD - 1:
                            release(mm)
                pe.wait_ge(sq_added, x_count + (KD + 1))
                mean_of(sq_sum).then_inc(sum_done, 1)
                chunk(0, 1)
                with pe.Fori(1, KF // 2) as i:
                    for r in range(2):
                        chunk(i, r)

            def release(mm):
                mm.then_inc(slot_used, 1)

            def down(layer, w, base_slot, phase):
                f0 = layer * (2 * KF) + w * KF
                with pe.Fori(0, KD // 4) as i:
                    for r in range(4):
                        if r == 0:
                            pe.wait_ge(f_ready, f0 + (KF - 1))
                            pe.wait_ge(g_scaled, f0 + (KF - 1))
                        if r == 2:
                            pe.wait_ge(g_scaled, f0 + KF)
                        pe.wait_ge(h_ready, updates(layer, phase) + 4 * i + (r - 3))
                        for part, n in enumerate(DOWN_TILES):
                            s = base_slot + 3 * r + part
                            low_in(layer, s, 12 * i)
                            def last_chunk(k):
                                if r == 0 and part == 2 and k == n - 1:
                                    pe.wait_ge(f_ready, f0 + KF)
                            mm = product(r, [(*tile_w(s, k), fh[:, 8 * part + k, :], fl[:, 8 * part + k, :]) for k in range(n)],
                                         first=part == 0, last=part == 2, before=last_chunk)
                            release(mm)

            def mixing(layer):
                slot = [ZIN]
                for step in MIX:
                    kind, arg = split(step)
                    p = psum_pair(step)
                    by_scalar, by_vector = tensor_needs(step)
                    if by_scalar:
                        act_did(pe, layer, max(by_scalar, key=ACT_STEPS.index))
                    if by_vector:
                        dve_did(pe, layer, max(by_vector, key=DVE_STEPS.index))
                    if step == "z:k":
                        pe.wait_ge(x_ready, updates(layer, 0) + 6)
                    if kind in ("z", "AB") or step == "qn:0":
                        low_in(layer, slot[0])
                        s = slot[0]
                        slot[0] += 1
                    if kind == "z":
                        if step == "z:kpe":
                            def tile_kpe(t, k):
                                return t[s % RING][:, k * C_ROPE:k * C_ROPE + P]
                            mm = product(p, [(tile_kpe(wh, k), tile_kpe(wl, k), xh[:, k, :], xl[:, k, :]) for k in range(KD)])
                        else:
                            before = None
                            if step == "z:k":
                                before = lambda k: pe.wait_ge(x_ready, updates(layer, 0) + (k + 1)) if k >= 6 else None
                            mm = product(p, x_tiles(s), before=before)
                    elif kind == "sumx":
                        pe.wait_ge(sq_added, updates(layer, 0) + (KD + 1))
                        mm = mean_of(sq_sum)
                    elif kind == "sumkv":
                        mm = mean_of(sq_sum)
                    elif kind == "sumq":
                        mm = mean_of(sq_tmp)
                    elif kind == "tw":
                        pe.wait_ge(mix_in, layer * N_MIX_IN + MIX_IN_FIRST)
                        for b in range(2):
                            nc.tensor.transpose(ps[p][:, 0, b * P:(b + 1) * P], wuk[:, 2 * b:2 * b + 2, :].rearrange("p h n -> p (h n)"), ident[:, :])
                        for g in range(A_GROUPS):
                            mm = nc.tensor.transpose(ps[p][:, 1, g * P:(g + 1) * P], ws[:, g, :], ident[:, :])
                    elif kind == "tc":
                        nc.tensor.transpose(ps[p][:, 0, 0:P], ck[:, :], ident[:, :])
                        for b in range(2):
                            nc.tensor.transpose(ps[p][:, 0, (1 + b) * P:(2 + b) * P], cckv[:, b, :], ident[:, :])
                        for b in range(2):
                            mm = nc.tensor.transpose(ps[p][:, 1, b * P:(b + 1) * P], ckpe4[:, b, :, :].rearrange("p c r -> p (c r)"), ident[:, :])
                    elif kind == "rep":
                        for half in range(2):
                            mm = nc.tensor.matmul(ps[p][:, half, 0:HALF], rep32[:, :], zs[0][0:C_ROPE, half * HALF:(half + 1) * HALF], start=True, stop=True)
                    elif kind == "rot":
                        src = {"k": zs[0], "q0": zs[1], "q1": zs[0], "q2": zs[1], "q3": zs[0], "kpe": kpe_rep, "qp": zs[1]}[arg]
                        if arg == "kpe":
                            pe.wait_ge(mix_in, layer * N_MIX_IN + N_MIX_IN)
                        m = rot64 if arg[0] == "k" and arg != "kpe" or arg in ("q0", "q1", "q2", "q3") else rot32
                        for half in range(2):
                            mm = nc.tensor.matmul(ps[p][:, half, 0:HALF], m[:, :], src[:, half * HALF:(half + 1) * HALF], start=True, stop=True)
                    elif kind in ("tv", "tckv", "tkpe", "tva"):
                        rows = C_ROPE if kind == "tkpe" else P
                        src = {"tv": vT, "tckv": ckvT, "tkpe": kpeT, "tva": zs[1 - arg] if kind == "tva" else None}[kind]
                        stand_alone(pe)
                        for t, (t0, n) in enumerate(TILES):
                            dst = ps[p][0:n, 0, t * rows:(t + 1) * rows] if t < 4 else ps[p][0:n, 1, 0:rows]
                            mm = nc.tensor.transpose(dst, src[0:rows, t0:t0 + n], ident[0:rows, 0:rows])
                    elif kind == "tk":
                        nc.tensor.transpose(ps[p][:, 0, 0:P], kT[:, 3 * P:4 * P], ident[:, :])
                        mm = nc.tensor.transpose(ps[p][0:DEC, 1, 0:P], kT[:, SEQ:NT], ident[:, :])
                    elif kind == "a":
                        for g in (2 * arg, 2 * arg + 1):
                            r = 64 * (g % 2)
                            c = slice(g * A_GDIM, (g + 1) * A_GDIM)
                            for t in range(4):
                                nc.tensor.matmul(ps[p][r:r + 64, 0, t * P:(t + 1) * P], va_tok[:, t, c], wsT[:, g, :], start=True, stop=True)
                            mm = nc.tensor.matmul(ps[p][r:r + 64, 1, 0:DEC], va_tok[0:DEC, 4, c], wsT[0:DEC, g, 0:DEC], start=True, stop=True)
                    elif kind == "qp":
                        off = KD * C_ROPE
                        mm = product(p, [(*tile_w(s, k, off), cqh[:, k, :], cql[:, k, :]) for k in range(KQ)])
                    elif kind == "qn":
                        mm = product(p, [(*tile_w(s, 2 * k + arg), cqh[:, k, :], cql[:, k, :]) for k in range(KQ)])
                    elif kind == "ql":
                        r = 64 * (arg % 2)
                        for half in range(2):
                            mm = nc.tensor.matmul(ps[p][:, half, 0:HALF], wukT[r:r + 64, arg // 2, :],
                                                  qnT[arg // 2][r:r + 64, half * HALF:(half + 1) * HALF], start=True, stop=True)
                    elif kind == "S":
                        i, g, t0, nq, keys = swa_unit(arg)
                        r = slice(64 * g, 64 * g + 64)
                        stand_alone(pe)
                        for j in range(B_GROUP):
                            col = 0
                            for tile, n in keys:
                                rhs = cT[r, 0:P] if tile < 0 else kT[r, tile * P:tile * P + n]
                                mm = nc.tensor.matmul(flat(p)[0:nq, j * 256 + col:j * 256 + col + n], qT[j][r, t0:t0 + nq], rhs, start=True, stop=True)
                                col += n
                    elif kind == "MS":
                        i, pair, t0, nq, keys = mla_unit(arg)
                        for j in range(2):
                            hd = 2 * pair + j
                            r = slice(32 * hd, 32 * hd + 32)
                            parts = [(cT[:, P:3 * P], ckpeT[r, :], 0, 2 * P), (ckvT[:, SEQ:NT], kpeT[r, SEQ:NT], 2 * P, DEC)] if i == 4 \
                                else [(ckvT[:, 0:(i + 1) * P], kpeT[r, 0:(i + 1) * P], 0, (i + 1) * P)]
                            for k_lat, k_pe, col, n in parts:
                                dst = ps[p][0:nq, j, col:col + n]
                                nc.tensor.matmul(dst, qlT[hd][:, t0:t0 + nq], k_lat, start=True, stop=False)
                                mm = nc.tensor.matmul(dst, qpT[r, t0:t0 + nq], k_pe, start=False, stop=True)
                    elif kind in ("T", "MT"):
                        i, g, t0, nq, keys = (swa_unit if kind == "T" else mla_unit)(arg)
                        heads, wide = (4, 256) if kind == "T" else (2, 512)
                        w = 512 if kind == "T" else 2 * nq
                        stand_alone(pe)
                        for k, (tile, n) in enumerate(keys):
                            for j in range(heads):
                                mm = nc.tensor.transpose(flat(p)[0:n, k * w + j * nq:k * w + (j + 1) * nq],
                                                         probs[0:nq, j * wide + k * P:j * wide + k * P + n], ident[0:nq, 0:nq])
                    elif kind == "O":
                        i, g, t0, nq, keys = swa_unit(arg)
                        r = slice(64 * g, 64 * g + 64)
                        for k, (tile, n) in enumerate(keys):
                            v = cv[:, r] if tile < 0 else v_tok[0:n, tile, r]
                            mm = nc.tensor.matmul(ps[p][r, 0, 0:4 * nq], v, probsT[arg % 2][0:n, k * 512:k * 512 + 4 * nq],
                                                  start=k == 0, stop=k == len(keys) - 1)
                    elif kind == "vc":
                        stand_alone(pe)
                        for n, t in enumerate(((0, 1, 2, 3), (4, 5, 6))[arg]):
                            keys = ckvT[:, t * P:(t + 1) * P] if t < 4 else cT[:, (t - 3) * P:(t - 2) * P] if t < 6 else ckvT[:, SEQ:NT]
                            rows = DEC if t == 6 else P
                            mm = nc.tensor.matmul(flat(p)[0:rows, n * 256:(n + 1) * 256], keys, wuv[:, :, :].rearrange("p h v -> p (h v)"), start=True, stop=True)
                    elif kind == "MO":
                        i, pair, t0, nq, keys = mla_unit(arg)
                        for j in range(2):
                            c = slice((2 * pair + j) * C_V, (2 * pair + j + 1) * C_V)
                            for k, (tile, n) in enumerate(keys):
                                row = tile if i < 4 else (4, 5, 6)[k]
                                mm = nc.tensor.matmul(ps[p][64 * j:64 * j + 64, 0, 0:nq], vc_tok[0:n, row, c],
                                                      probsT[arg % 2][0:n, (2 * k + j) * nq:(2 * k + j + 1) * nq],
                                                      start=k == 0, stop=k == len(keys) - 1)
                    elif kind == "AB":
                        mm = product(p, [(*tile_w(s, k), mh[:, k, :], ml[:, k, :]) for k in range(6)])
                    mm.then_inc(slot_used if step in SLOT_ENDS else pe_step, 1)

            def c_part(layer):
                for m in range(KD):
                    s, c = CC + m // 2, m % 2
                    if m == 0:
                        low_in(layer, s)
                        dve_did(pe, layer, "MO:9.0")
                        act_did(pe, layer, "MT:9.0")
                    elif c == 0:
                        low_in(layer, s)
                    if m >= 4:
                        pe.wait_ge(h_ready, updates(layer, 1) + (m - 3))
                    tiles = [(*tile_w(s, 2 * k + c), mh[:, 6 + k, :], ml[:, 6 + k, :]) for k in range(2)]
                    mm = product(m % 4, tiles)
                    mm.then_inc(slot_used if c else c_even_done, 1)

            pe.wait_ge(ident_in, 16)
            for m in range(KD):
                if m == 2:
                    pe.wait_ge(gain_rows_in, 6 * 16)
                    nc.tensor.transpose(ps[3][:, 1, 0:N_GAINS], g_rows[:, :], ident[0:N_GAINS, 0:N_GAINS]).then_inc(gains_T, 1)
                if m == 3:
                    pe.wait_ge(gains_ready, 1)
                if m >= 4:
                    pe.wait_ge(h_ready, m - 3)
                for t, (t0, n) in enumerate(TILES):
                    if t == 0 and m % (KD // 2) == 0:
                        pe.wait_ge(x_in[m // (KD // 2)], 32)
                    dst = ps[m % 4][:, 0, t * P:(t + 1) * P] if t < 4 else ps[m % 4][:, 1, 0:n]
                    mm = nc.tensor.transpose(dst, x_tok[0:n, t, m * P:(m + 1) * P], ident[0:n, 0:n])
                mm.then_inc(xT_done, 1)
            pe.wait_ge(consts_in, 3 * 16)

            with pe.Fori(0, DEPTH) as layer:
                gate_up(layer, 0, F1G, updates(layer, -1))
                down(layer, 0, F1D, 0)
                mixing(layer)
                c_part(layer)
                gate_up(layer, 1, F2G, updates(layer, 1))
                down(layer, 1, F2D, 2)

            pe.wait_ge(ident_made, DEPTH)
            last = updates(DEPTH, 0)
            def y_chunk(t, m):
                t0, n = TILES[t]
                dst = ps[t % 4][0:n, m // 4, (m % 4) * P:(m % 4 + 1) * P]
                nc.tensor.matmul(dst, xh[:, m, t0:t0 + n], ident_r[:, :], start=True, stop=False)
                return nc.tensor.matmul(dst, xl[:, m, t0:t0 + n], ident_r[:, :], start=False, stop=True)
            for t in range(3):
                pe.wait_ge(h_ready, last - 3 + t)
                if t == 0:
                    pe.wait_ge(x_ready, last - 1)
                for m in range(KD - 1):
                    y_chunk(t, m)
            pe.wait_ge(sq_added, last + 1)
            for t, (t0, n) in enumerate(TILES):
                mm = nc.tensor.matmul(ps[3][0:n, 0, t:t + 1], sq_sum[:, t0:t0 + n], mean_d[:, 0:1], start=True, stop=True)
            mm.then_inc(sum_done, 1)
            pe.wait_ge(x_ready, last)
            for t in range(3):
                y_chunk(t, KD - 1).then_inc(y_done, 1)
            for t in (3, 4):
                if t == 3:
                    pe.wait_ge(root_done, 2 * DEPTH + 2)
                else:
                    pe.wait_ge(y_left, 1)
                    pe.wait_ge(y_right, 1)
                for m in range(KD):
                    mm = y_chunk(t, m)
                mm.then_inc(y_done, 1)

        @block.vector
        def _(dve):
            def absorb_low(m, count, gain_col):
                gain = gains[:, gain_col:gain_col + 1] if isinstance(gain_col, int) else gains[:, bass.ds(gain_col, 1)]
                dve.wait_ge(h_ready, count + 1)
                dve.wait_ge(xh_ready, count + 1)
                nc.vector.scalar_tensor_tensor(out=xl[:, m, :], in0=h[:, m, :], scalar=gain, in1=xh[:, m, :].bitcast(F32),
                                               op0=ALU.mult, op1=ALU.subtract).then_inc(x_ready, 1)

            def add_square(count, square):
                dve.wait_ge(sq_made, count + 1)
                dve.wait_ge(sq_added, count + 1)
                nc.vector.tensor_tensor(sq_sum[:, :], sq_sum[:, :], square, ALU.add).then_inc(sq_added, 1)

            def add_squares(count):
                for m in range(KD):
                    add_square(count + m, squares[:, m, :])

            def add_out(m, p, scale):
                nc.vector.scalar_tensor_tensor(out=two_h(m), in0=halves(p), scalar=scale, in1=two_h(m),
                                               op0=ALU.mult, op1=ALU.add).then_inc(h_ready, 1)

            def two_h(m):
                if isinstance(m, int):
                    return two(h[:, m, :])
                return h[:, m, :].rearrange("p o (a n) -> p (o a) n", a=2)

            def clear_sum(count):
                nc.vector.memset(sq_sum[:, :], 0.0).then_inc(cleared, 1)
                dve.wait_ge(cleared, count + 1)
                stand_alone(dve)

            def make_rms(roots, count):
                dve.wait_ge(root_done, roots + 1)
                nc.vector.reciprocal(rms[:, :], rms[:, :]).then_inc(rms_ready, 1)
                dve.wait_ge(rms_ready, count + 1)

            def gate_up(layer, w):
                def chunk(i, r, first=False):
                    c = layer * (2 * KF) + 2 * i + (w * KF + r)
                    s = (F1G, F2G)[w] + 2 * r
                    if first:
                        make_rms(2 * layer + w, 3 * layer + 2 * w)
                    slot_done(dve, layer, s, 4 * i)
                    nc.vector.tensor_tensor(two(up[:, :]), halves(2 * r), two(rms[:, :]), ALU.mult).then_inc(up_scaled, 1)
                    slot_done(dve, layer, s + 1, 4 * i)
                    if not first:
                        dve.wait_ge(f_ready, c)
                    nc.vector.tensor_tensor(two(gate[:, :]), halves(2 * r + 1), two(rms[:, :]), ALU.mult).then_inc(g_scaled, 1)
                    dve.wait_ge(up_scaled, c + 1)
                    dve.wait_ge(silu_done, c + 1)
                    nc.vector.tensor_tensor(gate[:, :], gate[:, :], up[:, :], ALU.mult).then_inc(prod_ready, 1)
                    dve.wait_ge(prod_ready, c + 1)
                    dve.wait_ge(fh_ready, c + 1)
                    j = bass.ds(2 * i + r, 1)
                    nc.vector.tensor_tensor(fl[:, j, :], gate[:, :].unsqueeze(1), fh[:, j, :].bitcast(F32), ALU.subtract).then_inc(f_ready, 1)
                for r in range(2):
                    chunk(0, r, first=r == 0)
                with dve.Fori(1, KF // 2) as i:
                    for r in range(2):
                        chunk(i, r)

            def down(layer, phase, gain_base):
                clear_sum(3 * layer + phase)
                with dve.Fori(0, KD // 4) as i:
                    for r in range(4):
                        count = updates(layer, phase) + 4 * i + r
                        m = bass.ds(4 * i + r, 1)
                        slot_done(dve, layer, (F1D, F1D, F2D)[phase] + 3 * r + 2, 12 * i)
                        add_out(m, r, 0.5)
                        absorb_low(m, count, gain_base + 4 * i + r)
                        add_square(count, sq_tmp[:, :])

            def mixing(layer):
                emitted = [0]

                def emit(ins, name):
                    assert DVE_STEPS[emitted[0]] == name, (DVE_STEPS[emitted[0]], name)
                    emitted[0] += 1
                    ins.then_inc(dve_step, 1)

                def own(name):
                    dve_did(dve, layer, name)

                def adid(name):
                    act_did(dve, layer, name)

                def rows2(t):
                    return two(t[:, :])

                for step in MIX:
                    kind, arg = split(step)
                    p = psum_pair(step)
                    names = vector_ops(step)
                    if not names:
                        continue
                    if emitted[0]:
                        own(DVE_STEPS[emitted[0] - 1])
                    if kind not in ("sumx", "sumkv", "sumq", "tw", "rot"):
                        pe_did(dve, layer, step)
                    if kind == "z":
                        if arg == "k":
                            adid("sumx.0")
                            nc.vector.reciprocal(rms[:, :], rms[:, :]).then_inc(rms_ready, 1)
                            dve.wait_ge(rms_ready, 3 * layer + 2)
                        dst = {"k": zs[0], "v": vT, "q0": zs[1], "q1": zs[0], "q2": zs[1], "q3": zs[0], "va0": zs[1],
                               "va1": zs[0], "u0": uT[0], "u1": uT[1], "ckv": ckvT, "cq0": zs[1], "cq1": zs[0],
                               "cq2": zs[1], "kpe": zs[0]}[arg]
                        if arg in ("q1", "q2", "q3", "va0", "va1"):
                            pe_did(dve, layer, {"q1": "rot:k", "q2": "rot:q0", "q3": "rot:q1", "va0": "rot:q2", "va1": "rot:q3"}[arg])
                        if arg in ("cq0", "cq1"):
                            pe_did(dve, layer, f"tva:{arg[2]}")
                        emit(nc.vector.tensor_tensor(rows2(dst), halves(p), rows2(rms), ALU.mult), names[0])
                        if arg.startswith("cq"):
                            c = int(arg[2:])
                            adid(f"{step}.1")
                            own(names[0])
                            emit(nc.vector.scalar_tensor_tensor(out=cql[:, c, :], in0=dst[:, :], scalar=gains[:, bass.ds(layer * KQ + (G_Q + c), 1)],
                                                                in1=cqh[:, c, :].bitcast(F32), op0=ALU.mult, op1=ALU.subtract), names[1])
                            if c:
                                if c == 2:
                                    own("z:cq1.2")
                                emit(nc.vector.tensor_tensor(sq_tmp[:, :], sq_tmp[:, :], sq_sum[:, :], ALU.add), names[2])
                    elif kind == "sumx":
                        dve.wait_ge(mix_in, layer * N_MIX_IN + MIX_IN_FIRST)
                        emit(nc.vector.tensor_scalar(neg_sink[:, :], sinks[:, :], -1.0, None, ALU.mult), names[0])
                    elif kind == "sumkv":
                        adid("sumkv.0")
                        emit(nc.vector.reciprocal(rms_kv[:, :], rms_kv[:, :]), names[0])
                        own(names[0])
                        emit(nc.vector.scalar_tensor_tensor(out=ckvT[:, :], in0=ckvT[:, :], scalar=gains[:, bass.ds(layer + G_KV, 1)],
                                                            in1=rms_kv[:, :], op0=ALU.mult, op1=ALU.mult), names[1])
                    elif kind == "sumq":
                        adid("sumq.0")
                        emit(nc.vector.reciprocal(rms_q[:, :], rms_q[:, :]), names[0])
                        own(names[0])
                    elif kind == "tw":
                        adid("tw.1")
                        emit(nc.vector.memset(wsT[64:128, :, 0:64], 0.0), names[0])
                    elif kind == "rot":
                        src = {"k": zs[0], "q0": zs[1], "q1": zs[0], "q2": zs[1], "q3": zs[0], "kpe": kpe_rep, "qp": zs[1]}[arg]
                        dst = {"k": kT, "q0": qT[0], "q1": qT[1], "q2": qT[2], "q3": qT[3], "kpe": kpeT, "qp": qpT}[arg]
                        small = arg in ("kpe", "qp")
                        cos, sin = (cos32, sin32) if small else (cos64, sin64)
                        if arg != "kpe":
                            own("qp.0" if arg == "qp" else f"z:{arg}.0")
                        else:
                            adid("rep.0")
                            dve.wait_ge(mix_in, layer * N_MIX_IN + N_MIX_IN)
                        emit(nc.vector.tensor_tensor(dst[:, :], src[:, :], cos[:, :], ALU.mult), names[0])
                        pe_did(dve, layer, step)
                        emit(nc.vector.tensor_tensor(rows2(work), halves(p), rows2(sin), ALU.mult), names[1])
                        own(names[1])
                        emit(nc.vector.tensor_tensor(dst[:, :], dst[:, :], work[:, :], ALU.add), names[2])
                    elif kind == "a":
                        b = bias_a[:, arg, :]
                        emit(nc.vector.tensor_tensor(work[:, 0:SEQ].rearrange("p (t i) -> p t i", t=4), ps[p][:, 0, :].rearrange("p (t i) -> p t i", t=4),
                                                     b.unsqueeze(1).broadcast_to([P, 4, P]), ALU.add), names[0])
                        emit(nc.vector.tensor_tensor(work[:, SEQ:NT], ps[p][:, 1, 0:DEC], bias_a[:, arg, 0:DEC], ALU.add), names[1])
                        own(names[1])
                        emit(nc.vector.tensor_tensor(work[:, :], work[:, :], uT[arg][:, :], ALU.mult), names[2])
                        own(names[2])
                        adid(f"{step}.0")
                        emit(nc.vector.tensor_tensor(ml[:, arg, :], work[:, :], mh[:, arg, :].bitcast(F32), ALU.subtract), names[3])
                    elif kind == "qp":
                        pe_did(dve, layer, "z:kpe")
                        emit(nc.vector.tensor_tensor(rows2(zs[1]), halves(p), rows2(rms_q), ALU.mult), names[0])
                    elif kind == "qn":
                        emit(nc.vector.tensor_tensor(rows2(qnT[arg]), halves(p), rows2(rms_q), ALU.mult), names[0])
                    elif kind in ("S", "MS"):
                        swa = kind == "S"
                        i, g, t0, nq, keys = (swa_unit if swa else mla_unit)(arg)
                        heads, wide = (4, 256) if swa else (2, 512)
                        W = sum(n for _, n in keys)
                        sc = flat(p).rearrange("p (j w) -> p j w", w=wide)
                        n = 0
                        if i < 4:
                            emit(nc.vector.memset(sc[0:64, :, W - 64:W], NEG), names[n])
                            n += 1
                            if swa and i:
                                emit(nc.vector.memset(sc[64:128, :, 0:64], NEG), names[n])
                                n += 1
                            own(names[n - 1])
                        emit(nc.vector.tensor_reduce(top[0:nq, 0:heads], sc[0:nq, :, 0:W], AX_X, ALU.max), names[n])
                        own(names[n])
                        n += 1
                        if swa:
                            emit(nc.vector.scalar_tensor_tensor(out=neg_max[0:nq, :], in0=top[0:nq, :], scalar=-B_SCALE,
                                                                in1=neg_sink[0:nq, 4 * g:4 * g + 4], op0=ALU.mult, op1=ALU.min), names[n])
                            own(names[n])
                            n += 1
                            emit(nc.vector.tensor_tensor(sink_arg[0:nq, :], neg_max[0:nq, :], sinks[0:nq, 4 * g:4 * g + 4], ALU.add), names[n])
                            n += 1
                            adid(f"{step}.4")
                            emit(nc.vector.tensor_tensor(den_all[0:nq, :], den[0:nq, :], sink_exp[0:nq, :], ALU.add), names[n])
                            own(names[n])
                            n += 1
                            total = den_all
                        else:
                            emit(nc.vector.tensor_scalar(neg_max[0:nq, 0:2], top[0:nq, 0:2], -C_SCALE, None, ALU.mult), names[n])
                            n += 1
                            adid(f"{step}.1")
                            total = den
                        emit(nc.vector.reciprocal(inv_den[0:nq, 0:heads], total[0:nq, 0:heads]), names[n])
                        own(names[n])
                        n += 1
                        pr = probs[0:nq, :].rearrange("p (j w) -> p j w", w=wide)[:, :, 0:W]
                        inv = inv_den[0:nq, 0:heads].unsqueeze(2).broadcast_to([nq, heads, W])
                        if swa:
                            emit(nc.vector.tensor_tensor(pr[:, 0:2], pr[:, 0:2], inv[:, 0:2], ALU.mult), names[n])
                            n += 1
                            emit(nc.vector.tensor_tensor(pr[:, 2:4], pr[:, 2:4], inv[:, 2:4], ALU.mult), names[n])
                        else:
                            emit(nc.vector.tensor_tensor(pr, pr, inv, ALU.mult), names[n])
                    elif kind == "O":
                        i, g, t0, nq, keys = swa_unit(arg)
                        r = slice(64 * g, 64 * g + 64)
                        adid(f"{step}.0")
                        emit(nc.vector.tensor_tensor(ml[r, 2:6, t0:t0 + nq], ps[p][r, 0, 0:4 * nq].rearrange("p (j n) -> p j n", j=4),
                                                     mh[r, 2:6, t0:t0 + nq].bitcast(F32), ALU.subtract), names[0])
                    elif kind == "MO":
                        i, pair, t0, nq, keys = mla_unit(arg)
                        adid(f"{step}.0")
                        emit(nc.vector.tensor_tensor(ml[:, 6 + pair, t0:t0 + nq], ps[p][:, 0, 0:nq],
                                                     mh[:, 6 + pair, t0:t0 + nq].bitcast(F32), ALU.subtract), names[0])
                    elif kind == "AB":
                        emit(nc.vector.tensor_tensor(two_h(arg), halves(p), two_h(arg), ALU.add), names[0])
                assert emitted[0] == len(DVE_STEPS)

            nc.vector.memset(eps[:, :], EPS).then_inc(const_made, 1)
            nc.vector.memset(sq_sum[:, :], 0.0).then_inc(const_made, 1)
            nc.vector.memset(root_tok[:, :], 1.0).then_inc(const_made, 1)
            dve.sem_inc(sq_added, 1)
            dve.wait_ge(const_made, 3)
            for m in range(KD):
                dve.wait_ge(xT_done, m + 1)
                dve.wait_ge(h_part, m + 1)
                nc.vector.tensor_copy(h[:, m, 0:SEQ], ps[m % 4][:, 0, :]).then_inc(h_ready, 1)
                if m >= 1:
                    absorb_low(m - 1, m - 1, m - 1)
            absorb_low(KD - 1, KD - 1, KD - 1)
            add_squares(0)

            with dve.Fori(0, DEPTH) as layer:
                gate_up(layer, 0)
                down(layer, 0, layer * KD + G_MIX)
                mixing(layer)
                clear_sum(3 * layer + 1)
                count = updates(layer, 1)
                for m in range(KD):
                    if m == 0:
                        dve_did(dve, layer, "AB:7.0")
                    if m % 2:
                        slot_done(dve, layer, CC + m // 2)
                    else:
                        dve.wait_ge(c_even_done, layer * (KD // 2) + (m // 2 + 1))
                    add_out(m, m % 4, 1.0)
                    if m:
                        absorb_low(m - 1, count + (m - 1), layer * KD + (G_FFN2 + m - 1))
                absorb_low(KD - 1, count + (KD - 1), layer * KD + (G_FFN2 + KD - 1))
                add_squares(count)
                gate_up(layer, 1)
                dve.wait_ge(prod_ready, (layer + 1) * (2 * KF))
                nc.vector.tensor_copy(ident_r[:, :], ident[:, :]).then_inc(ident_made, 1)
                down(layer, 2, layer * KD + (G_FFN1 + KD))
            dve.wait_ge(root_done, 2 * DEPTH + 2)
            nc.vector.reciprocal(root_tok[:, :], root_tok[:, :]).then_inc(y_scale, 1)
            dve.wait_ge(y_scale, 1)
            for t, (t0, n) in enumerate(TILES):
                dve.wait_ge(y_done, t + 1)
                nc.vector.tensor_scalar(y_tok[0:n, t, 512:1024], ps[t % 4][0:n, 1, :], root_tok[0:n, t:t + 1], None, ALU.mult).then_inc(y_right, 1)


_INS = ["x_prompt", "x_sample", "cache_swa_k", "cache_swa_v", "cache_mla_ckv", "cache_mla_kpe",
        "norm_ffn1", "w1_gate", "w1_up", "w1_down", "norm_mix", "w_in", "cm_w_s", "cm_b", "swa_sink",
        "mla_norm_q", "mla_w_uq", "mla_w_uk", "mla_w_uv", "mla_norm_kv", "w_out",
        "norm_ffn2", "w2_gate", "w2_up", "w2_down", "norm_final"]
_OUTS = [(1, SEQ, D_MODEL), (1, DEC, D_MODEL),
         (DEPTH, 1, WINDOW, B_KV_HEADS, B_DIM), (DEPTH, 1, WINDOW, B_KV_HEADS, B_DIM),
         (DEPTH, 1, SEQ, C_KV), (DEPTH, 1, SEQ, C_ROPE),
         (DEPTH, 1, DEC, B_KV_HEADS, B_DIM), (DEPTH, 1, DEC, B_KV_HEADS, B_DIM),
         (DEPTH, 1, DEC, C_KV), (DEPTH, 1, DEC, C_ROPE), (DEPTH, 1, DEC, A_WIDTH)]


def matrices():
    out = np.zeros((5, P, P), np.float32)
    out[0] = np.eye(P)
    for n, d in ((1, B_DIM), (2, C_ROPE)):
        for m in range(P):
            first = m % d < d // 2
            out[n, m + d // 2 if first else m - d // 2, m] = -1.0 if first else 1.0
    out[3] = 1.0 / D_MODEL
    out[4, :C_ROPE] = np.tile(np.eye(C_ROPE), 4)
    return out


def rope_tables():
    pos = np.concatenate([np.arange(SEQ), PAST + np.arange(DEC)]).astype(np.float32)
    out = []
    for d in (B_DIM, C_ROPE):
        half = d // 2
        inv = np.float32(10000.0) ** (np.float32(-2.0) * np.arange(half, dtype=np.float32) / np.float32(d))
        ang = inv.astype(np.float32)[:, None] * pos[None, :]
        for f in (np.cos, np.sin):
            out.append(np.tile(f(ang).astype(np.float32), (P // half, 1)))
    return np.stack(out)


def kernel(**inputs):
    import numpy as _np
    import concourse.bacc as _bacc
    from concourse import mybir as _mybir
    from concourse.bass_utils import run_bass_kernel_spmd as _run

    nc = _bacc.Bacc("TRN2", target_bir_lowering=False, num_devices=1)
    arrays, args = {}, {}
    given = {name: inputs[name] for name in _INS}
    given["const"], given["rope"] = matrices(), rope_tables()
    for name, value in given.items():
        v = _np.ascontiguousarray(value)
        arrays[f"in_{name}_dram"] = v
        args[name] = nc.dram_tensor(f"in_{name}_dram", v.shape, _mybir.dt.from_np(v.dtype), kind="ExternalInput").ap()
    outs = [nc.dram_tensor(f"out_{i}_dram", shape, _mybir.dt.float32, kind="ExternalOutput").ap()
            for i, shape in enumerate(_OUTS)]
    build(nc, args, outs)
    r = _run(nc, [arrays], core_ids=[0])
    return tuple(r.results[0][f"out_{i}_dram"] for i in range(len(_OUTS)))
```
